# Optimizing a Trainium2 kernel written in Bass

```python
import math
import jax
import jax.numpy as jnp
from jax import lax
import numpy as np

D_MODEL = 2048
BATCH = 1
SEQ = 256
DEPTH = 2

D_FF = 4 * D_MODEL
CONV_A_WIDTH = D_MODEL // 2
CONV_A_K = 3
FOX_HEADS = 8
FOX_HEAD_DIM = (D_MODEL // 2) // FOX_HEADS
FOX_WIDTH = FOX_HEADS * FOX_HEAD_DIM
FOX_Q_BLOCK = 128
AB_IN = 3 * CONV_A_WIDTH + 3 * FOX_WIDTH + FOX_HEADS
AB_SPLITS = (CONV_A_WIDTH, CONV_A_WIDTH, CONV_A_WIDTH, FOX_WIDTH, FOX_WIDTH, FOX_WIDTH, FOX_HEADS)
GDN_HEAD_DIM = 128
GDN_QK_HEADS = D_MODEL // GDN_HEAD_DIM
GDN_V_HEADS = 2 * GDN_QK_HEADS
GDN_K_WIDTH = GDN_QK_HEADS * GDN_HEAD_DIM
GDN_V_WIDTH = GDN_V_HEADS * GDN_HEAD_DIM
GDN_QKV = 2 * GDN_K_WIDTH + GDN_V_WIDTH
GDN_IN = GDN_QKV + GDN_V_WIDTH + 2 * GDN_V_HEADS
GDN_CONV_K = 4
GDN_CHUNK = 64
N_EVEN = (DEPTH + 1) // 2
N_ODD = DEPTH // 2
NORM_EPS = 1e-6

kernel_name = "hybrid_conv_fox_gdn_trunk"

def _split(t, sizes):
    idx = [int(s) for s in np.cumsum(sizes)[:-1]]
    return jnp.split(t, idx, axis=-1)

def rms_norm(x, g):
    xf = x.astype(jnp.float32)
    y = xf * lax.rsqrt(jnp.mean(xf * xf, axis=-1, keepdims=True) + NORM_EPS) * g.astype(jnp.float32)
    return y.astype(x.dtype)

def l2_norm(x):
    xf = x.astype(jnp.float32)
    return xf * lax.rsqrt(jnp.sum(xf * xf, axis=-1, keepdims=True) + NORM_EPS)

def causal_depthwise_conv(u, w):
    k_width = w.shape[-1]
    rhs = jnp.transpose(w)[:, None, :].astype(u.dtype)
    return lax.conv_general_dilated(
        u, rhs, window_strides=(1,), padding=[(k_width - 1, 0)],
        dimension_numbers=("NWC", "WIO", "NWC"), feature_group_count=u.shape[-1])

def forgetting_attention(q, k, v, log_f):
    bsz, s_len, n_h, d = q.shape
    nb = s_len // FOX_Q_BLOCK
    c = jnp.cumsum(log_f.astype(jnp.float32), axis=1).transpose(0, 2, 1)
    q_blocks = q.reshape(bsz, nb, FOX_Q_BLOCK, n_h, d).transpose(1, 0, 3, 2, 4)
    c_blocks = c.reshape(bsz, n_h, nb, FOX_Q_BLOCK).transpose(2, 0, 1, 3)
    kh = k.transpose(0, 2, 1, 3)
    vh = v.transpose(0, 2, 1, 3)
    k_pos = jnp.arange(s_len)
    scale = d ** -0.5

    def block(args):
        q_blk, c_blk, blk_idx = args
        q_pos = blk_idx * FOX_Q_BLOCK + jnp.arange(FOX_Q_BLOCK)
        logits = (jnp.einsum("bhqd,bhkd->bhqk", q_blk, kh).astype(jnp.float32) * scale
                  + c_blk[..., :, None] - c[:, :, None, :])
        logits = jnp.where(k_pos[None, :] <= q_pos[:, None], logits, -jnp.inf)
        p = jax.nn.softmax(logits, axis=-1)
        return jnp.einsum("bhqk,bhkd->bhqd", p.astype(vh.dtype), vh)

    o = lax.map(block, (q_blocks, c_blocks, jnp.arange(nb)))
    return o.transpose(1, 0, 3, 2, 4).reshape(bsz, s_len, n_h * d)

def conv_fox_mixer(h, w_in, conv_w, f_bias, q_norm, k_norm, w_out):
    bsz, s_len, _ = h.shape
    proj = h @ w_in
    gate_b, gate_c, xv, q, k, v, f_logit = _split(proj, AB_SPLITS)
    y_a = gate_b * causal_depthwise_conv(gate_c * xv, conv_w)
    q = rms_norm(q.reshape(bsz, s_len, FOX_HEADS, FOX_HEAD_DIM), q_norm)
    k = rms_norm(k.reshape(bsz, s_len, FOX_HEADS, FOX_HEAD_DIM), k_norm)
    v = v.reshape(bsz, s_len, FOX_HEADS, FOX_HEAD_DIM)
    log_f = jax.nn.log_sigmoid(f_logit.astype(jnp.float32) + f_bias.astype(jnp.float32))
    y_b = forgetting_attention(q, k, v, log_f).astype(h.dtype)
    return jnp.concatenate([y_a, y_b], axis=-1) @ w_out

def gated_delta_rule_chunked(q, k, v, g, beta):
    f32 = jnp.float32
    bsz, s_len, n_h, dk = q.shape
    dv = v.shape[-1]
    csz = GDN_CHUNK
    n = s_len // csz

    def to_chunks(t):
        t = t.reshape((bsz, n, csz, n_h) + t.shape[3:])
        return jnp.moveaxis(t, 1, 0).swapaxes(2, 3)

    qc = to_chunks(q.astype(f32) * dk ** -0.5)
    kc = to_chunks(k.astype(f32))
    vc = to_chunks(v.astype(f32))
    bc = to_chunks(beta.astype(f32))
    gc = jnp.cumsum(to_chunks(g.astype(f32)), axis=-1)
    incl = jnp.tril(jnp.ones((csz, csz), dtype=bool))
    strict = jnp.tril(jnp.ones((csz, csz), dtype=bool), -1)
    diff = gc[..., :, None] - gc[..., None, :]
    decay = jnp.where(incl, jnp.exp(jnp.where(incl, diff, 0.0)), 0.0)
    kb = kc * bc[..., None]
    lower = jnp.where(strict, jnp.einsum("nbhcd,nbhsd->nbhcs", kb, kc) * decay, 0.0)
    eye = jnp.eye(csz, dtype=f32)
    t_inv = lax.linalg.triangular_solve(lower + eye, jnp.broadcast_to(eye, lower.shape),
                                        left_side=True, lower=True, unit_diagonal=True)
    u = jnp.einsum("nbhcs,nbhse->nbhce", t_inv, vc * bc[..., None])
    w = jnp.einsum("nbhcs,nbhsd->nbhcd", t_inv, kb * jnp.exp(gc)[..., None])

    def step(state, inp):
        q_i, k_i, u_i, w_i, g_i, dec_i = inp
        v_new = u_i - jnp.einsum("bhcd,bhde->bhce", w_i, state)
        scores = jnp.einsum("bhcd,bhsd->bhcs", q_i, k_i) * dec_i
        o_i = (jnp.einsum("bhcd,bhde->bhce", q_i * jnp.exp(g_i)[..., None], state)
               + jnp.einsum("bhcs,bhse->bhce", scores, v_new))
        g_last = g_i[..., -1:]
        state = (state * jnp.exp(g_last)[..., None]
                 + jnp.einsum("bhcd,bhce->bhde", k_i * jnp.exp(g_last - g_i)[..., None], v_new))
        return state, o_i

    state0 = jnp.zeros((bsz, n_h, dk, dv), f32)
    _, o = lax.scan(step, state0, (qc, kc, u, w, gc, decay))
    return jnp.moveaxis(o.swapaxes(2, 3), 0, 1).reshape(bsz, s_len, n_h, dv)

def gated_deltanet_mixer(h, w_in, conv_w, a_log, dt_bias, out_norm, w_out):
    bsz, s_len, _ = h.shape
    proj = h @ w_in
    qkv, z, b, a = _split(proj, (GDN_QKV, GDN_V_WIDTH, GDN_V_HEADS, GDN_V_HEADS))
    qkv = jax.nn.silu(causal_depthwise_conv(qkv, conv_w))
    q, k, v = _split(qkv, (GDN_K_WIDTH, GDN_K_WIDTH, GDN_V_WIDTH))
    rep = GDN_V_HEADS // GDN_QK_HEADS
    q = jnp.repeat(l2_norm(q.reshape(bsz, s_len, GDN_QK_HEADS, GDN_HEAD_DIM)), rep, axis=2)
    k = jnp.repeat(l2_norm(k.reshape(bsz, s_len, GDN_QK_HEADS, GDN_HEAD_DIM)), rep, axis=2)
    v = v.reshape(bsz, s_len, GDN_V_HEADS, GDN_HEAD_DIM)
    beta = jax.nn.sigmoid(b.astype(jnp.float32))
    g = -jnp.exp(a_log.astype(jnp.float32)) * jax.nn.softplus(a.astype(jnp.float32) + dt_bias.astype(jnp.float32))
    o = gated_delta_rule_chunked(q, k, v, g, beta)
    z = z.reshape(bsz, s_len, GDN_V_HEADS, GDN_HEAD_DIM).astype(jnp.float32)
    o = rms_norm(o, out_norm) * jax.nn.silu(z)
    return o.reshape(bsz, s_len, GDN_V_WIDTH).astype(h.dtype) @ w_out

def sqrelu_mlp(h, w1, w2):
    return jnp.square(jax.nn.relu(h @ w1)) @ w2

def setup_inputs(seed: int = 0) -> dict:
    key = jax.random.key(seed)
    ks = jax.random.split(key, 17)
    f32 = jnp.float32

    def normal(k, shape, scale):
        return jax.random.normal(k, shape, f32) * scale

    def gain(k, shape):
        return 1.0 + 0.02 * jax.random.normal(k, shape, f32)

    x = normal(ks[0], (BATCH, SEQ, D_MODEL), 1.0)
    norm_mix = gain(ks[1], (DEPTH, D_MODEL))
    norm_mlp = gain(ks[2], (DEPTH, D_MODEL))
    w_mlp_in = normal(ks[3], (DEPTH, D_MODEL, D_FF), D_MODEL ** -0.5)
    w_mlp_out = normal(ks[4], (DEPTH, D_FF, D_MODEL), D_FF ** -0.5)
    ab_w_in = normal(ks[5], (N_EVEN, D_MODEL, AB_IN), D_MODEL ** -0.5)
    ab_conv_w = normal(ks[6], (N_EVEN, CONV_A_WIDTH, CONV_A_K), CONV_A_K ** -0.5)
    fox_f_bias = jax.random.uniform(ks[7], (N_EVEN, FOX_HEADS), f32, 1.0, 5.0)
    fox_q_norm = gain(ks[8], (N_EVEN, FOX_HEAD_DIM))
    fox_k_norm = gain(ks[9], (N_EVEN, FOX_HEAD_DIM))
    ab_w_out = normal(ks[10], (N_EVEN, CONV_A_WIDTH + FOX_WIDTH, D_MODEL), (CONV_A_WIDTH + FOX_WIDTH) ** -0.5)
    gdn_w_in = normal(ks[11], (N_ODD, D_MODEL, GDN_IN), D_MODEL ** -0.5)
    gdn_conv_w = normal(ks[12], (N_ODD, GDN_QKV, GDN_CONV_K), GDN_CONV_K ** -0.5)
    gdn_a_log = jnp.log(jax.random.uniform(ks[13], (N_ODD, GDN_V_HEADS), f32, 1.0, 16.0))
    dt = jnp.exp(jax.random.uniform(ks[14], (N_ODD, GDN_V_HEADS), f32, math.log(1e-3), math.log(1e-1)))
    gdn_dt_bias = dt + jnp.log(-jnp.expm1(-dt))
    gdn_out_norm = gain(ks[15], (N_ODD, GDN_HEAD_DIM))
    gdn_w_out = normal(ks[16], (N_ODD, GDN_V_WIDTH, D_MODEL), GDN_V_WIDTH ** -0.5)
    return {
        "x": x, "norm_mix": norm_mix, "norm_mlp": norm_mlp,
        "w_mlp_in": w_mlp_in, "w_mlp_out": w_mlp_out,
        "ab_w_in": ab_w_in, "ab_conv_w": ab_conv_w, "fox_f_bias": fox_f_bias,
        "fox_q_norm": fox_q_norm, "fox_k_norm": fox_k_norm, "ab_w_out": ab_w_out,
        "gdn_w_in": gdn_w_in, "gdn_conv_w": gdn_conv_w, "gdn_a_log": gdn_a_log,
        "gdn_dt_bias": gdn_dt_bias, "gdn_out_norm": gdn_out_norm, "gdn_w_out": gdn_w_out,
    }

def reference(x, norm_mix, norm_mlp, w_mlp_in, w_mlp_out, ab_w_in, ab_conv_w, fox_f_bias,
              fox_q_norm, fox_k_norm, ab_w_out, gdn_w_in, gdn_conv_w, gdn_a_log,
              gdn_dt_bias, gdn_out_norm, gdn_w_out):
    for layer in range(DEPTH):
        i = layer // 2
        h = rms_norm(x, norm_mix[layer])
        if layer % 2 == 0:
            x = x + conv_fox_mixer(h, ab_w_in[i], ab_conv_w[i], fox_f_bias[i],
                                   fox_q_norm[i], fox_k_norm[i], ab_w_out[i])
        else:
            x = x + gated_deltanet_mixer(h, gdn_w_in[i], gdn_conv_w[i], gdn_a_log[i],
                                         gdn_dt_bias[i], gdn_out_norm[i], gdn_w_out[i])
        h = rms_norm(x, norm_mlp[layer])
        x = x + sqrelu_mlp(h, w_mlp_in[layer], w_mlp_out[layer])
    return x


_drawn_inputs = setup_inputs


def setup_inputs(seed=0):
    import zlib

    import numpy as np

    out = dict(_drawn_inputs(seed))
    spreads = {}
    factors = {'fox_q_norm': 8.0, 'fox_k_norm': 8.0, 'gdn_out_norm': 8.0}
    for name, (base, spread) in spreads.items():
        noise = np.random.default_rng([zlib.crc32(name.encode()), seed]).standard_normal(out[name].shape)
        drawn = base * np.exp(spread * noise) if base else spread * noise
        out[name] = jnp.asarray(drawn.astype(out[name].dtype))
    for name, factor in factors.items():
        out[name] = (out[name] * factor).astype(out[name].dtype)
    return out
```

```python
from contextlib import ExitStack, contextmanager

import numpy as np

import concourse.bass as bass
from concourse import mybir

ALU = mybir.AluOpType
ACT = mybir.ActivationFunctionType
F32 = mybir.dt.float32
F32R = mybir.dt.float32r
AX_X = mybir.AxisListType.X

P = 128
SEQ = 256
TT = SEQ // P
D = 2048
KT = D // P
D_FF = 4 * D
CONV_A = 1024
FOX_HEADS = 8
HD = 128
QK_HEADS, V_HEADS = 16, 32
GROUPS = 4
GQ = QK_HEADS // GROUPS
GV = V_HEADS // GROUPS
GDN_K, GDN_V = QK_HEADS * HD, V_HEADS * HD
EPS = 1e-6
NEG = -1e30
LEVELS = (2, 4, 8, 16, 32, 64)

SETUP_LOADS, LATE_LOADS = 6, 8
PER_GROUP = 8 * 3 + GQ * 5
PIECE = 1024
UNIT = 2 * PIECE
RAW = 4
SPLIT = 4
BODY = 8
BLOCKS = D_FF // D
TILES = 24

CONSTS = ["ident", "upper", "ones", "decay_mask", "zero", "causal_mask", "sub1", "sub1_t"] + [f"sub{b}" for b in LEVELS]


def shape_constants():
    r, c = np.arange(P)[:, None], np.arange(P)[None, :]

    def sub(b):
        return ((r // (2 * b) == c // (2 * b)) & (r // b % 2 == 1) & (c // b % 2 == 0)).astype(np.float32)

    made = {
        "ident": (r == c), "upper": (r <= c), "ones": (r >= 0) & (c >= 0), "zero": (r < 0) & (c < 0),
        "decay_mask": np.where(r <= c, 0.0, NEG), "causal_mask": np.where(c <= r, 0.0, NEG),
        "sub1": sub(1), "sub1_t": sub(1).T,
    }
    made |= {f"sub{b}": sub(b) for b in LEVELS}
    return np.ascontiguousarray(np.stack([np.asarray(made[n], np.float32) for n in CONSTS], axis=1))


def trunk(nc, x_in, norm_mix, norm_mlp, w_mlp_in, w_mlp_out, ab_w_in, ab_conv_w, fox_f_bias, fox_q_norm,
          fox_k_norm, ab_w_out, gdn_w_in, gdn_conv_w, gdn_a_log, gdn_dt_bias, gdn_out_norm, gdn_w_out,
          consts_in, out):
    with ExitStack() as ctx:
        def sb(name, shape, dt=F32):
            return ctx.enter_context(nc.sbuf_tensor("sb_" + name, [P] + shape, dt))

        def sem(name):
            return ctx.enter_context(nc.semaphore(name))

        raw = sb("raw", [RAW, UNIT])
        wh = sb("wh", [SPLIT, PIECE], F32R)
        wl = sb("wl", [SPLIT, PIECE], F32R)
        x = sb("x", [TT, D])
        hx = sb("hx", [KT, 2, SEQ], F32R)
        yx = sb("yx", [KT, 2, SEQ], F32R)
        proj = sb("proj", [TILES, SEQ])
        scratch = sb("scratch", [7304])
        cst = sb("cst", [len(CONSTS), P])
        gains = sb("gains", [4, KT])
        cw_a = sb("cw_a", [8, 3])
        cw_g = sb("cw_g", [64, 4])
        cw_grp = sb("cw_grp", [2 * GQ + GV, 4])
        small = sb("small", [96])
        stats = sb("stats", [8])
        fcols = sb("fcols", [2, TT, FOX_HEADS])
        gcols = sb("gcols", [5, TT, V_HEADS])
        gg = sb("gg", [5, TT, GV])

        def const(name):
            return cst[:, CONSTS.index(name), :]

        ident, upper, ones = const("ident"), const("upper"), const("ones")
        causal2 = cst[:, CONSTS.index("zero"):CONSTS.index("causal_mask") + 1, :].rearrange("p a c -> p (a c)")

        psum = ctx.enter_context(nc.psum_tensor("psum", [P, 8, 512], F32))
        acc = [psum[:, i, :] for i in range(4)]
        bank = [psum[:, 4 + i, :] for i in range(4)]

        loaded = [sem(f"loaded{i}") for i in range(RAW)]
        high_done, low_done, used = sem("high_done"), sem("low_done"), sem("used")
        rest_out, evacuated = sem("rest_out"), sem("evacuated")

        block = ctx.enter_context(nc.Block())

        at = {"piece": 0, "cg": 0}
        phases = {}

        def phase(name, bodies, form):
            phases[name] = (at["piece"], at["cg"])
            at["piece"] += bodies * BODY * (2 if form == "B" else 1)
            at["cg"] += bodies * 2

        phase("conv_in", 6, "A")
        phase("fox_in", 6, "A")
        phase("ab_out", 2, "B")
        MLP_P, MLP_C = 4 * BODY + 2 * 2 * BODY, 4 * 2 + 2 * 2
        GRP_P, GRP_C = 6 * BODY, 6 * 2
        HALF_P, HALF_C = 2 * GRP_P + 2 * 2 * BODY, 2 * GRP_C + 2 * 2

        def mlp_phase(n):
            phases[f"mlp{n}"] = (at["piece"], at["cg"])
            at["piece"] += BLOCKS * MLP_P
            at["cg"] += BLOCKS * MLP_C

        mlp_phase(0)
        phases["gdn"] = (at["piece"], at["cg"])
        at["piece"] += 2 * HALF_P
        at["cg"] += 2 * HALF_C
        mlp_phase(1)
        PIECES = at["piece"]

        def rows(w):
            return w.rearrange("(t p) n -> p t n", p=P)

        setup_loaded = sem("setup_loaded")
        small_w_loaded, small_low_done = sem("small_w_loaded"), sem("small_low_done")
        late_loaded, stored = sem("late_loaded"), sem("stored")

        SMALL_N = 2 * V_HEADS
        small_w = scratch[:, 5500:5500 + KT * SMALL_N].rearrange("p (t n) -> p t n", t=KT)
        yx_flat = yx[:].rearrange("p t a s -> p (t a s)")
        small_h = yx_flat[:, 0:KT * SMALL_N].rearrange("p (t n) -> p t n", t=KT)
        small_l = yx_flat[:, KT * SMALL_N:2 * KT * SMALL_N].rearrange("p (t n) -> p t n", t=KT)
        nrows = scratch[:, 1024:1024 + P]

        @block.sync
        def _(sp):
            def unit(p0, s, src, form, first=False):
                if not first:
                    sp.wait_ge(high_done, p0 + 2 * s - 2 * RAW + 2)
                    sp.wait_ge(low_done, p0 + 2 * s - 2 * RAW + 2)
                kt, w = (8, 256) if form == "A" else (4, 512)
                dst = raw[:, s % RAW, :].rearrange("p (t n) -> p t n", t=kt)
                sp.dma_start(dst, src).then_inc(loaded[s % RAW], 16)

            def body_a(p0, w, col, first=False):
                for s in range(4):
                    unit(p0, s, w[:, s % 2 * 8:s % 2 * 8 + 8, bass.ds(col + s // 2 * 256, 256)], "A", first)

            def body_b(p0, w, t0, col):
                for s in range(8):
                    unit(p0, s, w[:, bass.ds(t0 + s % 4 * 4, 4), bass.ds(col + s // 4 * 512, 512)], "B")

            sp.dma_start(x[:], x_in[0].rearrange("(t p) d -> p t d", p=P)).then_inc(setup_loaded, 16)
            sp.dma_start(cst[:], consts_in).then_inc(setup_loaded, 16)
            for n, g in enumerate((norm_mix, norm_mlp)):
                for layer in range(2):
                    r0 = KT * (2 * layer + n)
                    sp.dma_start(nrows[r0:r0 + KT, :], g[layer].rearrange("(t p) -> t p", p=P)).then_inc(setup_loaded, 16)
            ab = rows(ab_w_in[0])
            body_a(0, ab, 0, first=True)
            with nc.allow_non_contiguous_dma(reason="per-channel constants, loaded once"):
                sp.dma_start(cw_a[:], ab_conv_w[0].rearrange("(t p) k -> p t k", p=P)).then_inc(late_loaded, 16)
                sp.dma_start(cw_g[:], gdn_conv_w[0].rearrange("(t p) k -> p t k", p=P)).then_inc(late_loaded, 16)
                for i, v in enumerate((fox_q_norm, fox_k_norm, gdn_out_norm)):
                    sp.dma_start(small[:, i:i + 1], v.rearrange("a d -> d a")).then_inc(late_loaded, 16)
            sp.dma_start(small[:, 8:16], fox_f_bias.to_broadcast([P, FOX_HEADS])).then_inc(late_loaded, 16)
            sp.dma_start(small[:, 16:48], gdn_a_log.to_broadcast([P, V_HEADS])).then_inc(late_loaded, 16)
            sp.dma_start(small[:, 48:80], gdn_dt_bias.to_broadcast([P, V_HEADS])).then_inc(late_loaded, 16)
            sp.dma_start(small_w[:, :, 0:FOX_HEADS], ab[:, :, 3 * CONV_A + 3 * FOX_HEADS * HD:]).then_inc(small_w_loaded, 16)
            with sp.Fori(1, 6) as i:
                body_a(i * BODY, ab, i * 512)
            with sp.Fori(0, 6) as i:
                body_a(i * BODY + phases["fox_in"][0], ab, i * 512 + 3 * CONV_A)
            wo = rows(ab_w_out[0])
            with sp.Fori(0, 2) as i:
                body_b(i * 2 * BODY + phases["ab_out"][0], wo, 0, i * 1024)

            def mlp(layer):
                w1, w2 = rows(w_mlp_in[layer]), rows(w_mlp_out[layer])
                base = phases[f"mlp{layer}"][0]
                with sp.Fori(0, BLOCKS) as b:
                    with sp.Fori(0, 4) as i:
                        body_a(b * MLP_P + i * BODY + base, w1, b * D + i * 512)
                    with sp.Fori(0, 2) as i:
                        body_b(b * MLP_P + i * 2 * BODY + (base + 4 * BODY), w2, b * KT, i * 1024)

            mlp(0)
            wg, wgo = rows(gdn_w_in[0]), rows(gdn_w_out[0])
            sp.wait_ge(small_low_done, 1)
            sp.dma_start(small_w, wg[:, :, 2 * GDN_K + 2 * GDN_V:]).then_inc(small_w_loaded, 16)
            with sp.Fori(0, 2) as half:
                with sp.Fori(0, 2) as g2:
                    p0 = half * HALF_P + g2 * GRP_P + phases["gdn"][0]
                    g = half * 2 + g2
                    body_a(p0, wg, g * 512)
                    body_a(p0 + BODY, wg, g * 512 + GDN_K)
                    for n in range(4):
                        body_a(p0 + (2 + n) * BODY, wg, g * 1024 + (2 * GDN_K if n < 2 else 2 * GDN_K + GDN_V) + n % 2 * 512)
                with sp.Fori(0, 2) as i:
                    body_b(half * HALF_P + i * 2 * BODY + (phases["gdn"][0] + 2 * GRP_P), wgo, half * KT, i * 1024)
            mlp(1)
            sp.wait_ge(evacuated, at["cg"])
            sp.dma_start(out[0].rearrange("(t p) d -> p t d", p=P), x[:]).then_inc(stored, 16)
            sp.wait_ge(stored, 16)

        def high(act, p, slot_unit_wait, k, first=False):
            act.wait_ge(loaded[k // 2 % RAW], slot_unit_wait)
            if not first:
                act.wait_ge(used, p - SPLIT + 1)
            nc.scalar.activation(wh[:, k % SPLIT, :], raw[:, k // 2 % RAW, k % 2 * PIECE:(k % 2 + 1) * PIECE],
                                 ACT.Copy).then_inc(high_done, 1)

        def low(dve, p, k):
            dve.wait_ge(high_done, p + 1)
            nc.vector.tensor_tensor(wl[:, k % SPLIT, :], raw[:, k // 2 % RAW, k % 2 * PIECE:(k % 2 + 1) * PIECE],
                                    wh[:, k % SPLIT, :].bitcast(F32), ALU.subtract).then_inc(low_done, 1)

        def stream_act(act, p0, k, ahead=SPLIT):
            q = k + ahead
            high(act, p0 + q, p0 * 2 + 16 * (q // BODY + 1), q % BODY)

        def stream_dve(dve, p0, k):
            low(dve, p0 + k + SPLIT, (k + SPLIT) % BODY)

        def last_piece(p0, k):
            return isinstance(p0, int) and p0 + k + SPLIT >= PIECES

        def pe_a(pe, p0, cg0, src, first=False):
            for k in range(BODY):
                banks = acc[k // 4 * 2:k // 4 * 2 + 2]
                if k % 4 == 0 and not first:
                    pe.wait_ge(evacuated, cg0 + k // 4 - 1)
                pe.wait_ge(low_done, p0 + k + 1)
                h, l = (t[:, k % SPLIT, :].rearrange("p (t n) -> p t n", t=4) for t in (wh, wl))
                for t in range(4):
                    kt = k % 4 * 4 + t
                    for n in range(2):
                        cols = slice(n * P, (n + 1) * P)
                        nc.tensor.matmul(banks[n], h[:, t, cols], src[:, kt, :, :].rearrange("p a s -> p (a s)"),
                                         start=kt == 0, stop=False, skip_group_check=True)
                        mm = nc.tensor.matmul(banks[n][:, SEQ:2 * SEQ], l[:, t, cols], src[:, kt, 0, :],
                                              start=False, stop=kt == KT - 1, skip_group_check=True)
                mm.then_inc(used, 1)

        def pe_b(pe, p0, cg0, src):
            for k in range(2 * BODY):
                banks = acc[k // BODY * 2:k // BODY * 2 + 2]
                if k % BODY == 0:
                    pe.wait_ge(evacuated, cg0 + k // BODY - 1)
                pe.wait_ge(low_done, p0 + k + 1)
                h, l = (t[:, k % SPLIT, :].rearrange("p (t n) -> p t n", t=2) for t in (wh, wl))
                for t in range(2):
                    kt = k % BODY * 2 + t
                    for n in range(TT):
                        toks = slice(n * P, (n + 1) * P)
                        nc.tensor.matmul(banks[n], src[:, kt, 0, toks], h[:, t, :], start=kt == 0, stop=False)
                        nc.tensor.matmul(banks[n], src[:, kt, 0, toks], l[:, t, :], start=False, stop=False)
                        mm = nc.tensor.matmul(banks[n], src[:, kt, 1, toks], h[:, t, :], start=False, stop=kt == KT - 1)
                mm.then_inc(used, 1)

        def act_body(act, p0, pieces, evac=None, end=False):
            for k in range(pieces):
                if not (end and k + SPLIT >= pieces):
                    q = k + SPLIT
                    high(act, p0 + q, p0 * 2 + 16 * (q // BODY + 1), q % BODY)
                if evac and k % 4 == 3:
                    evac(k // 4)

        def dve_body(dve, p0, cg0, pieces, per_group, evac, end=False):
            for k in range(pieces):
                if not (end and k + SPLIT >= pieces):
                    low(dve, p0 + k + SPLIT, (k + SPLIT) % BODY)
                if k % per_group == per_group - 1:
                    dve.wait_ge(used, p0 + k + 1)
                    evac(k // per_group)

        a_groups = {"conv_in": 0, "fox_in": 12, "mlp0": 24, "gdn": 24 + 8 * BLOCKS, "mlp1": 72 + 8 * BLOCKS}

        def rest_to(act, g, p, dst):
            act.wait_ge(used, p + 1)
            nc.scalar.activation(dst, psum[:, 2 * g:2 * g + 2, SEQ:2 * SEQ], ACT.Copy).then_inc(rest_out, 1)

        def sum_to(dve, g, count, dst):
            dve.wait_ge(rest_out, count)
            nc.vector.tensor_tensor(dst, psum[:, 2 * g:2 * g + 2, 0:SEQ], dst, ALU.add).then_inc(evacuated, 1)

        names = ["gain_rows_turned", "gains_ready", "x_squared", "mean_ready", "rstd_ready", "x_scaled", "norm_turned",
                 "norm_high", "norm_low",
                 "small_high", "small_done", "gate_args", "gate_exps", "gate_rates", "gate_sums", "gate_exp2", "gates_ready",
                 "vector_order", "scalar_order", "squared", "mlp_high", "mlp_low", "zeroed",
                 "pads_zeroed", "conv_out", "conv_high", "conv_low",
                 "qk_squared", "qk_sums", "qk_roots", "qk_ready", "v_staged", "v_turned", "v_ready", "logit_rows", "logits_done",
                 "max_ready", "exps_done", "probs_ready", "probs_turned", "probs_out", "fox_out", "fox_high", "fox_low",
                 "convolved", "scores_ready", "activated", "group_cols", "g_spread", "sums_spread", "decay_args", "decays_ready",
                 "grams_done", "lower_ready", "lower_turned", "inverse_ready", "product_done", "product_masked",
                 "update_done", "turns_ready", "u0_done", "u0_ready", "state_done", "state_ready", "read_done",
                 "rhs1_ready", "u1_done", "u1_ready", "o_done", "o_squared", "o_sums", "o_roots", "y_ready", "y_high", "y_low"]
        S = {n: sem(n) for n in names}

        class Order:

            def __init__(self, eng, name):
                self.eng, self.sem, self.n, self.per = eng, S[name], 0, 0

            def __call__(self, ins):
                self.n, self.per = self.n + 1, self.per + 1
                ins.then_inc(self.sem, 1)
                self.eng.wait_ge(self.sem, self.n)

            @contextmanager
            def passes(self, start, end, count):
                before, per = self.n, self.per
                with self.eng.Fori(start, end) as i:
                    self.n, self.per = before + (i - start) * count, 0
                    yield i
                    assert self.per == count, (self.per, count)
                self.n, self.per = before + (end - start) * count, per + (end - start) * count

        def view(t, o, shape):
            n = int(np.prod(shape))
            v = t[:, o:o + n]
            if len(shape) == 1:
                return v
            names_ = "abcd"[:len(shape)]
            return v.rearrange(f"p ({' '.join(names_)}) -> p {' '.join(names_)}", **dict(zip(names_, shape)))

        xs = proj[:, 0:KT, :].rearrange("p t s -> p (t s)").rearrange("p (t d) -> p t d", t=TT)
        mlp_sum = view(scratch, 0, [2, 2, SEQ])
        mlp_sq = view(scratch, 1024, [2, 2, SEQ])
        conv_u = view(scratch, 1280, [8, 258])
        conv_y = view(scratch, 1280 + 8 * 258, [8, SEQ])
        f_sq = view(scratch, 0, [2, SEQ])
        f_rt = view(scratch, 512, [2, SEQ])
        f_qk = view(scratch, 1024, [2, SEQ])
        f_v = view(scratch, 1536, [SEQ])
        f_lf = view(scratch, 1792, [TT, P])
        f_lg = view(scratch, 2048, [3, P])
        f_p = view(scratch, 2432, [3, P])
        f_pt = view(scratch, 2816, [3, P])
        f_vt = view(scratch, 3200, [TT, P])
        f_st = view(scratch, 3456, [16])
        fcols_flat = fcols[:].rearrange("p a t h -> p (a t h)")
        cw_a_flat = cw_a[:].rearrange("p t k -> p (t k)")
        psum_flat = psum[:].rearrange("p b n -> p (b n)")
        g_t = view(scratch, 3500, [6, TT, V_HEADS])
        d_u = view(scratch, 6784, [2, 260])
        d_sq, d_rt, d_qk = (view(scratch, 512 * i, [2, SEQ]) for i in range(3))
        d_gb, d_df, d_D, d_Lt, d_T, d_Tt, d_Y, d_Sc, d_Vt = (view(scratch, 1536 + 512 * i, [2, TT, P]) for i in range(9))
        d_qe = view(scratch, 1536 + 512 * 9, [2, P])
        d_Kt = view(scratch, 1536 + 512 * 9 + 256, [P])
        d_S = view(scratch, 1536 + 512 * 9 + 384, [2, P])
        d_c = d_T.rearrange("p a b c -> p (a b c)").rearrange("p (a s) -> p a s", a=2)
        d_vn = d_gb
        d_R, d_vs = d_df[:, 0], d_df[:, 1]
        d_y = d_sq
        q_bias, k_bias = small[:, 80:81], small[:, 1:2]
        eps_col = small[:, 82:83]
        G, BETA, NEGC, NEGEXP, BLAST = range(5)

        @block.tensor
        def _(pe):
            def norm(n, cg):
                for p in range(8):
                    pe.wait_ge(S["x_scaled"], 2 * n + 2)
                    if p >= 4:
                        pe.wait_ge(S["norm_low"], KT * n + 2 * (p - 4) + 2)
                    for j in range(2):
                        for t in range(TT):
                            mm = nc.tensor.transpose(bank[p % 4][:, j * SEQ + t * P:j * SEQ + (t + 1) * P],
                                                     xs[:, t, (2 * p + j) * P:(2 * p + j + 1) * P], ident)
                    mm.then_inc(S["norm_turned"], 1)
                pe.wait_ge(S["norm_low"], KT * (n + 1))

            def small_proj(n, width):
                pe.wait_ge(small_low_done, n + 1)
                for t in range(TT):
                    o = bank[0][:, t * SMALL_N:t * SMALL_N + width]
                    toks = slice(t * P, (t + 1) * P)
                    for kt in range(KT):
                        nc.tensor.matmul(o, hx[:, kt, 0, toks], small_h[:, kt, 0:width], start=kt == 0, stop=False)
                        nc.tensor.matmul(o, hx[:, kt, 0, toks], small_l[:, kt, 0:width], start=False, stop=False)
                        mm = nc.tensor.matmul(o, hx[:, kt, 1, toks], small_h[:, kt, 0:width], start=False, stop=kt == KT - 1)
                mm.then_inc(S["small_done"], 1)

            pe.wait_ge(setup_loaded, 16 * SETUP_LOADS)
            nc.tensor.transpose(bank[0][:, 0:64], nrows[0:64, :], ident[0:64, 0:64]).then_inc(S["gain_rows_turned"], 1)
            norm(0, 0)
            small_proj(0, FOX_HEADS)
            pe.wait_ge(S["gate_rates"], 1)
            nc.tensor.matmul(bank[1][:, 0:8], upper, fcols[:, 0, 0, :], start=True, stop=True)
            nc.tensor.matmul(bank[1][:, 8:16], ones, fcols[:, 0, 0, :], start=True, stop=False)
            nc.tensor.matmul(bank[1][:, 8:16], upper, fcols[:, 0, 1, :], start=False, stop=True).then_inc(S["gate_sums"], 1)

            pe_a(pe, 0, 0, hx, first=True)
            with pe.Fori(1, 6) as i:
                pe_a(pe, i * BODY, i * 2, hx)
            with pe.Fori(0, 6) as i:
                pe_a(pe, i * BODY + phases["fox_in"][0], i * 2 + phases["fox_in"][1], hx)
            pe.wait_ge(evacuated, phases["ab_out"][1])
            with pe.Fori(0, FOX_HEADS) as h:
                pe.wait_ge(S["qk_squared"], h + 1)
                nc.tensor.matmul(bank[0], ones, f_sq.rearrange("p a s -> p (a s)"), start=True, stop=True).then_inc(S["qk_sums"], 1)
                pe.wait_ge(S["v_staged"], h + 1)
                for t in range(TT):
                    mm = nc.tensor.transpose(bank[1][:, t * P:(t + 1) * P], f_v[:, t * P:(t + 1) * P], ident)
                mm.then_inc(S["v_turned"], 1)
                pe.wait_ge(S["qk_ready"], h + 1)
                pe.wait_ge(S["logit_rows"], h + 1)
                nc.tensor.matmul(bank[2][:, 0:P], f_qk[:, 0, 0:P], f_qk[:, 1, 0:P], start=True, stop=False)
                nc.tensor.matmul(bank[2][:, 0:P], f_lf[:, 0, :], upper, start=False, stop=True)
                nc.tensor.matmul(bank[2][:, P:2 * P], f_qk[:, 0, P:SEQ], f_qk[:, 1, 0:P], start=True, stop=False)
                nc.tensor.matmul(bank[2][:, P:2 * P], f_lf[:, 0, :], upper, start=False, stop=True)
                nc.tensor.matmul(bank[2][:, 2 * P:3 * P], f_qk[:, 0, P:SEQ], f_qk[:, 1, P:SEQ], start=True, stop=False)
                nc.tensor.matmul(bank[2][:, 2 * P:3 * P], f_lf[:, 0, :], ones, start=False, stop=False)
                nc.tensor.matmul(bank[2][:, 2 * P:3 * P], f_lf[:, 1, :], upper, start=False,
                                 stop=True).then_inc(S["logits_done"], 1)
                pe.wait_ge(S["probs_ready"], h + 1)
                for i in range(3):
                    mm = nc.tensor.transpose(bank[3][:, i * P:(i + 1) * P], f_p[:, i, :], ident)
                mm.then_inc(S["probs_turned"], 1)
                pe.wait_ge(S["probs_out"], h + 1)
                pe.wait_ge(S["v_ready"], h + 1)
                nc.tensor.matmul(bank[0][:, 0:P], f_vt[:, 0, :], f_pt[:, 0, :], start=True, stop=True)
                nc.tensor.matmul(bank[0][:, P:SEQ], f_vt[:, 0, :], f_pt[:, 1, :], start=True, stop=False)
                nc.tensor.matmul(bank[0][:, P:SEQ], f_vt[:, 1, :], f_pt[:, 2, :], start=False,
                                 stop=True).then_inc(S["fox_out"], 1)
                pe.wait_ge(S["fox_low"], h + 1)
            pe.wait_ge(S["conv_low"], 1)
            with pe.Fori(0, 2) as i:
                pe_b(pe, i * 2 * BODY + phases["ab_out"][0], i * 2 + phases["ab_out"][1], yx)

            def mlp(layer):
                base, cg = phases[f"mlp{layer}"]
                norm(2 * layer + 1, cg)
                with pe.Fori(0, BLOCKS) as b:
                    with pe.Fori(0, 4) as i:
                        pe_a(pe, b * MLP_P + i * BODY + base, b * MLP_C + i * 2 + cg, hx)
                    with pe.Fori(0, 2) as i:
                        pe.wait_ge(S["mlp_low"], b * 8 + (2 + 8 * (BLOCKS * layer + 1)))
                        pe_b(pe, b * MLP_P + i * 2 * BODY + (base + 4 * BODY), b * MLP_C + i * 2 + (cg + 8), yx)

            mlp(0)
            gp, gc = phases["gdn"]
            norm(2, gc)
            small_proj(1, SMALL_N)
            pe.wait_ge(S["gate_rates"], 2)
            gflat = gcols[:, G].rearrange("p t h -> p (t h)")
            nc.tensor.matmul(bank[1][:, 0:64], upper, gflat, start=True, stop=True)
            nc.tensor.matmul(bank[1][:, 64:128], ones, gflat, start=True, stop=True).then_inc(S["gate_sums"], 1)


            def head(n, j):
                pe.wait_ge(S["qk_squared"], n + (1 + FOX_HEADS))
                nc.tensor.matmul(bank[0], ones, d_sq.rearrange("p a s -> p (a s)"), start=True, stop=True).then_inc(S["qk_sums"], 1)
                pe.wait_ge(S["g_spread"], n + 1)
                for m in range(4):
                    mm = nc.tensor.matmul(bank[1][:, m * P:(m + 1) * P], d_gb[:, m // 2, m % 2, :], upper, start=True, stop=True)
                mm.then_inc(S["sums_spread"], 1)
                pe.wait_ge(S["qk_ready"], n + (1 + FOX_HEADS))
                for t in range(TT):
                    kk, qk = (bank[3][:, (2 * t + i) * P:(2 * t + i + 1) * P] for i in range(2))
                    toks = slice(t * P, (t + 1) * P)
                    nc.tensor.matmul(kk, d_qk[:, 1, toks], d_qk[:, 1, toks], start=True, stop=True)
                    mm = nc.tensor.matmul(qk, d_qk[:, 1, toks], d_qk[:, 0, toks], start=True, stop=True)
                mm.then_inc(S["grams_done"], 1)
                for e in range(2):
                    for t in range(TT):
                        m = 2 * e + t
                        nc.tensor.transpose(bank[2][:, m * P:(m + 1) * P], proj[:, 8 + 2 * j + e, t * P:(t + 1) * P], ident)
                nc.tensor.transpose(bank[0][:, 0:P], d_qk[:, 1, 0:P], ident).then_inc(S["v_turned"], 1)
                pe.wait_ge(S["lower_ready"], n + 1)
                for m in range(4):
                    mm = nc.tensor.transpose(bank[1][:, m * P:(m + 1) * P], d_Lt[:, m // 2, m % 2, :], ident)
                mm.then_inc(S["lower_turned"], 1)
                pe.wait_ge(S["turns_ready"], n + 1)
                pe.wait_ge(S["scores_ready"], n + 1)
                for i in range(len(LEVELS)):
                    pe.wait_ge(S["inverse_ready"], n * 7 + (i + 1))
                    for m in range(4):
                        mm = nc.tensor.matmul(bank[2][:, m * P:(m + 1) * P], d_Lt[:, m // 2, m % 2, :],
                                              d_T[:, m // 2, m % 2, :], start=True, stop=True)
                    mm.then_inc(S["product_done"], 1)
                    pe.wait_ge(S["product_masked"], n * 6 + (i + 1))
                    for m in range(4):
                        if i < len(LEVELS) - 1:
                            nc.tensor.matmul(bank[0][:, m * P:(m + 1) * P], d_Tt[:, m // 2, m % 2, :],
                                             d_Y[:, m // 2, m % 2, :], start=True, stop=True)
                        mm = nc.tensor.matmul(bank[3][:, m * P:(m + 1) * P], d_Y[:, m // 2, m % 2, :],
                                              d_Tt[:, m // 2, m % 2, :], start=True, stop=True)
                    mm.then_inc(S["update_done"], 1)
                pe.wait_ge(S["inverse_ready"], n * 7 + 7)
                for e in range(2):
                    mm = nc.tensor.matmul(bank[1][:, e * P:(e + 1) * P], d_Tt[:, e, 0, :], d_Vt[:, e, 0, :], start=True, stop=True)
                mm.then_inc(S["u0_done"], 1)
                pe.wait_ge(S["u0_ready"], n + 1)
                for e in range(2):
                    mm = nc.tensor.matmul(bank[2][:, e * P:(e + 1) * P], d_Kt, d_vs[:, e, :], start=True, stop=True)
                mm.then_inc(S["state_done"], 1)
                pe.wait_ge(S["state_ready"], n + 1)
                for e in range(2):
                    mm = nc.tensor.matmul(bank[0][:, e * P:(e + 1) * P], d_qk[:, 1, P:SEQ], d_S[:, e, :], start=True, stop=True)
                mm.then_inc(S["read_done"], 1)
                pe.wait_ge(S["rhs1_ready"], n + 1)
                for e in range(2):
                    mm = nc.tensor.matmul(bank[1][:, (2 + e) * P:(3 + e) * P], d_Tt[:, e, 1, :], d_R[:, e, :], start=True, stop=True)
                mm.then_inc(S["u1_done"], 1)
                pe.wait_ge(S["u1_ready"], n + 1)
                for e in range(2):
                    o = [bank[3][:, (2 * e + t) * P:(2 * e + t + 1) * P] for t in range(TT)]
                    nc.tensor.matmul(o[0], d_vn[:, e, 0, :], d_Sc[:, e, 0, :], start=True, stop=True)
                    nc.tensor.matmul(o[1], d_vn[:, e, 1, :], d_Sc[:, e, 1, :], start=True, stop=False)
                    mm = nc.tensor.matmul(o[1], d_S[:, e, :], d_qe[:, e, :], start=False, stop=True)
                mm.then_inc(S["o_done"], 1)
                pe.wait_ge(S["o_squared"], n + 1)
                nc.tensor.matmul(bank[2], ones, d_rt.rearrange("p a s -> p (a s)"), start=True, stop=True).then_inc(S["o_sums"], 1)

            with pe.Fori(0, 2) as half:
                with pe.Fori(0, 2) as g2:
                    for b in range(6):
                        pe_a(pe, half * HALF_P + g2 * GRP_P + (gp + b * BODY), half * HALF_C + g2 * GRP_C + (gc + 2 * b), hx)
                    pe.wait_ge(S["activated"], half * 24 + g2 * 12 + 13)
                    for j in range(GQ):
                        head(half * (2 * GQ) + g2 * GQ + j, j)
                with pe.Fori(0, 2) as i:
                    pe.wait_ge(S["y_low"], half * (2 * GQ) + 2 * GQ)
                    pe_b(pe, half * HALF_P + i * 2 * BODY + (gp + 2 * GRP_P), half * HALF_C + i * 2 + (gc + 2 * GRP_C), yx)
            mlp(1)

        @block.scalar
        def _(act):
            order = Order(act, "scalar_order")

            def copy(out, in_, scale=1.0):
                return nc.scalar.activation(out, in_, ACT.Copy, scale=scale)

            def norm(n, cg):
                if n == 0:
                    act.wait_ge(setup_loaded, 16 * SETUP_LOADS)
                else:
                    act.wait_ge(evacuated, cg)
                for t in range(TT):
                    sq = nc.scalar.activation(xs[:, t, :], x[:, t, :], ACT.Square, accum_out=stats[:, t:t + 1])
                sq.then_inc(S["x_squared"], 1)
                if n == 0:
                    act.wait_ge(S["gains_ready"], 1)
                for p in range(8):
                    act.wait_ge(S["norm_turned"], 8 * n + p + 1)
                    for j in range(2):
                        copy(hx[:, 2 * p + j, 0, :], bank[p % 4][:, j * SEQ:(j + 1) * SEQ],
                             gains[:, n, 2 * p + j:2 * p + j + 1]).then_inc(S["norm_high"], 1)

            def small_high_parts(n, width):
                act.wait_ge(small_w_loaded, 16 * (n + 1))
                copy(small_h[:, :, 0:width], small_w[:, :, 0:width]).then_inc(S["small_high"], 1)

            for p in range(SPLIT):
                high(act, p, 16, p, first=True)
            norm(0, 0)
            small_high_parts(0, FOX_HEADS)
            act.wait_ge(S["gate_args"], 1)
            e = g_t[:, 3, :, 0:FOX_HEADS]
            order(nc.scalar.activation(e, e, ACT.Exp))
            nc.scalar.activation(e, e, ACT.Ln, bias=1.0).then_inc(S["gate_exps"], 1)

            def proj_rest(p0, i):
                return lambda g: rest_to(act, g, p0 + 4 * g + 3, proj[:, bass.ds(i * 4 + 2 * g, 2), :])

            act_body(act, 0, BODY, proj_rest(0, 0))
            with act.Fori(1, 6) as i:
                act_body(act, i * BODY, BODY, proj_rest(i * BODY, i))
            act.wait_ge(S["conv_out"], 1)
            with act.Fori(0, 6) as i:
                p0 = i * BODY + phases["fox_in"][0]
                act_body(act, p0, BODY, proj_rest(p0, i))
            copy(yx[:, 0:8, 0, :], conv_y).then_inc(S["conv_high"], 1)
            act.wait_ge(evacuated, phases["ab_out"][1])
            act.wait_ge(S["conv_low"], 1)
            heads = proj[:].rearrange("p (a h) s -> p a h s", a=3)
            with act.Fori(0, FOX_HEADS) as h:
                nc.scalar.activation(f_sq.unsqueeze(2), heads[:, 0:2, bass.ds(h, 1), :], ACT.Square).then_inc(S["qk_squared"], 1)
                copy(f_v.unsqueeze(1), heads[:, 2, bass.ds(h, 1), :]).then_inc(S["v_staged"], 1)
                act.wait_ge(S["qk_sums"], h + 1)
                nc.scalar.activation(f_rt.rearrange("p a s -> p (a s)"), bank[0], ACT.Sqrt, scale=1.0 / HD,
                                     bias=eps_col).then_inc(S["qk_roots"], 1)
                act.wait_ge(S["v_turned"], h + 1)
                copy(f_vt.rearrange("p t c -> p (t c)"), bank[1][:, 0:SEQ]).then_inc(S["v_ready"], 1)
                act.wait_ge(S["max_ready"], h + 1)
                nc.scalar.activation(f_p[:, 0, :], f_lg[:, 0, :], ACT.Exp, bias=f_st[:, 2:3], accum_out=f_st[:, 4:5])
                nc.scalar.activation(f_p[:, 1:3, :], f_lg[:, 1:3, :], ACT.Exp, bias=f_st[:, 3:4],
                                     accum_out=f_st[:, 5:6]).then_inc(S["exps_done"], 1)
                act.wait_ge(S["probs_turned"], h + 1)
                copy(f_pt.rearrange("p i c -> p (i c)"), bank[3][:, 0:3 * P]).then_inc(S["probs_out"], 1)
                act.wait_ge(S["fox_out"], h + 1)
                copy(yx[:, bass.ds(h + 8, 1), 0, :], bank[0][:, 0:SEQ].unsqueeze(1)).then_inc(S["fox_high"], 1)
            with act.Fori(0, 2) as i:
                act_body(act, i * 2 * BODY + phases["ab_out"][0], 2 * BODY)

            def mlp(layer):
                base, cg = phases[f"mlp{layer}"]
                norm(2 * layer + 1, cg)

                def block_(b, end=False):
                    with act.Fori(0, 4) as i:
                        p0 = b * MLP_P + i * BODY + base

                        def evac(g):
                            rest_to(act, g, p0 + 4 * g + 3, mlp_sum[:, g])
                            act.wait_ge(S["squared"], b * 8 + i * 2 + (8 * BLOCKS * layer + g + 1))
                            copy(yx[:, bass.ds(i * 4 + 2 * g, 2), 0, :], mlp_sq[:, g]).then_inc(S["mlp_high"], 1)

                        act_body(act, p0, BODY, evac)
                    def down(i, end=False):
                        act_body(act, b * MLP_P + i * 2 * BODY + (base + 4 * BODY), 2 * BODY, end=end)

                    if end:
                        down(0)
                        down(1, True)
                    else:
                        with act.Fori(0, 2) as i:
                            down(i)

                with act.Fori(0, BLOCKS - 1) as b:
                    block_(b)
                block_(BLOCKS - 1, end=layer == 1)

            mlp(0)
            gp, gc = phases["gdn"]
            norm(2, gc)
            small_high_parts(1, SMALL_N)
            act.wait_ge(S["gate_args"], 2)
            order(nc.scalar.activation(g_t[:, 3:5], g_t[:, 3:5], ACT.Exp))
            order(nc.scalar.activation(small[:, 16:48], small[:, 16:48], ACT.Exp))
            nc.scalar.activation(g_t[:, 3], g_t[:, 3], ACT.Ln, bias=1.0).then_inc(S["gate_exps"], 1)
            act.wait_ge(S["gate_args"], 3)
            nc.scalar.activation(g_t[:, 1].rearrange("p t h -> p (t h)"), bank[1][:, 0:64], ACT.Exp)
            nc.scalar.activation(g_t[:, 0], g_t[:, 0], ACT.Exp).then_inc(S["gate_exp2"], 1)
            copy(stats[:, 6:7], stats[:, 0:1]).then_inc(S["activated"], 1)

            def head(n, j, yt):
                tiles = proj[:, 0:8, :].rearrange("p (a t) s -> p a t s", a=2)
                nc.scalar.activation(d_sq, tiles[:, :, j, :], ACT.Square).then_inc(S["qk_squared"], 1)
                act.wait_ge(S["qk_sums"], n + (1 + FOX_HEADS))
                nc.scalar.activation(d_rt.rearrange("p a s -> p (a s)"), bank[0], ACT.Sqrt, bias=eps_col).then_inc(S["qk_roots"], 1)
                act.wait_ge(S["decay_args"], n + 1)
                nc.scalar.activation(d_D, d_df, ACT.Exp)
                act.wait_ge(S["sums_spread"], n + 1)
                nc.scalar.activation(d_qe, bank[1].rearrange("p (e t c) -> p e t c", e=2, t=2)[:, :, 1, :],
                                     ACT.Exp).then_inc(S["decays_ready"], 1)
                act.wait_ge(S["v_turned"], n + (1 + FOX_HEADS))
                copy(d_Vt.rearrange("p e t c -> p (e t c)"), bank[2])
                copy(d_Kt, bank[0][:, 0:P]).then_inc(S["turns_ready"], 1)
                act.wait_ge(S["u0_done"], n + 1)
                for e in range(2):
                    u = bank[1][:, e * P:(e + 1) * P]
                    c = 2 * j + e
                    copy(d_vn[:, e, 0, :], u, gg[:, BETA, 0, c:c + 1])
                    last = copy(d_vs[:, e, :], u, gg[:, BLAST, 0, c:c + 1])
                last.then_inc(S["u0_ready"], 1)
                act.wait_ge(S["state_done"], n + 1)
                copy(d_S, bank[2][:, 0:2 * P].rearrange("p (e c) -> p e c", e=2)).then_inc(S["state_ready"], 1)
                act.wait_ge(S["u1_done"], n + 1)
                for e in range(2):
                    last = copy(d_vn[:, e, 1, :], bank[1][:, (2 + e) * P:(3 + e) * P], gg[:, BETA, 1, 2 * j + e:2 * j + e + 1])
                last.then_inc(S["u1_ready"], 1)
                act.wait_ge(S["o_done"], n + 1)
                nc.scalar.activation(d_rt.rearrange("p a s -> p (a s)"), bank[3], ACT.Square).then_inc(S["o_squared"], 1)
                act.wait_ge(S["o_sums"], n + 1)
                nc.scalar.activation(d_rt.rearrange("p a s -> p (a s)"), bank[2], ACT.Sqrt, scale=1.0 / HD,
                                     bias=eps_col).then_inc(S["o_roots"], 1)
                act.wait_ge(S["y_ready"], n + 1)
                copy(yx[:, bass.ds(yt, 2), 0, :], d_y).then_inc(S["y_high"], 1)
                act.wait_ge(S["y_low"], n + 1)

            with act.Fori(0, 2) as half:
                with act.Fori(0, 2) as g2:
                    for b in range(6):
                        p0 = half * HALF_P + g2 * GRP_P + (gp + b * BODY)

                        def evac(g):
                            if b >= 4:
                                act.wait_ge(S["activated"], half * 24 + g2 * 12 + 2 * b + g + 1)
                            rest_to(act, g, p0 + 4 * g + 3, d_u[:, :, 3:259] if b < 4 else d_c)
                            if b < 4:
                                act.wait_ge(S["convolved"], half * 16 + g2 * 8 + 2 * b + g + 1)
                            else:
                                act.wait_ge(evacuated, half * HALF_C + g2 * GRP_C + (gc + 2 * b + g + 1))
                            nc.scalar.activation(proj[:, 4 * b + 2 * g:4 * b + 2 * g + 2, :], d_c, ACT.Silu).then_inc(S["activated"], 1)

                        act_body(act, p0, BODY, evac)
                    act.wait_ge(S["activated"], half * 24 + g2 * 12 + 13)
                    for j in range(GQ):
                        head(half * (2 * GQ) + g2 * GQ + j, j, g2 * 8 + 2 * j)
                with act.Fori(0, 2) as i:
                    act_body(act, half * HALF_P + i * 2 * BODY + (gp + 2 * GRP_P), 2 * BODY)
            mlp(1)

        @block.vector
        def _(dve):
            tt, ts, stt = nc.vector.tensor_tensor, nc.vector.tensor_scalar, nc.vector.scalar_tensor_tensor
            order = Order(dve, "vector_order")

            def norm(n):
                dve.wait_ge(S["x_squared"], n + 1)
                ts(stats[:, 2:4], stats[:, 0:2], 1.0 / D, EPS, ALU.mult, ALU.add).then_inc(S["mean_ready"], 1)
                dve.wait_ge(S["rstd_ready"], n + 1)
                for t in range(TT):
                    ts(xs[:, t, :], x[:, t, :], stats[:, 4 + t:5 + t], None, ALU.mult).then_inc(S["x_scaled"], 1)
                for p in range(8):
                    dve.wait_ge(S["norm_high"], KT * n + 2 * p + 2)
                    for j in range(2):
                        kt = 2 * p + j
                        stt(hx[:, kt, 1, :], bank[p % 4][:, j * SEQ:(j + 1) * SEQ], gains[:, n, kt:kt + 1],
                            hx[:, kt, 0, :].bitcast(F32), ALU.mult, ALU.subtract).then_inc(S["norm_low"], 1)

            def small_low_parts(n, width):
                dve.wait_ge(S["small_high"], n + 1)
                tt(small_l[:, :, 0:width], small_w[:, :, 0:width], small_h[:, :, 0:width].bitcast(F32),
                   ALU.subtract).then_inc(small_low_done, 1)

            def out_proj(p0, cg0, i, end=False):
                def evac(g):
                    for t in range(TT):
                        cols = x[:, t, bass.ds(i * 1024 + g * 512, 512)]
                        last = tt(cols, cols, acc[2 * g + t], ALU.add)
                    last.then_inc(evacuated, 1)

                dve_body(dve, p0, cg0, 2 * BODY, BODY, evac, end)

            for p in range(SPLIT):
                low(dve, p, p)
            dve.wait_ge(S["gain_rows_turned"], 1)
            nc.vector.tensor_copy(gains[:].rearrange("p n t -> p (n t)"), bank[0][:, 0:64]).then_inc(S["gains_ready"], 1)
            norm(0)
            small_low_parts(0, FOX_HEADS)
            dve.wait_ge(late_loaded, 16 * LATE_LOADS)
            order(ts(q_bias, small[:, 0:1], HD ** -0.5, None, ALU.mult))
            dve.wait_ge(S["small_done"], 1)
            t0, t1, t2, t3 = (g_t[:, i, :, 0:FOX_HEADS] for i in range(4))
            for t in range(TT):
                last = tt(t0[:, t], bank[0][:, t * SMALL_N:t * SMALL_N + FOX_HEADS], small[:, 8:16], ALU.add)
            order(last)
            order(ts(t1, t0, -1.0, None, ALU.mult))
            ts(t2, t1, 0.0, None, ALU.max)
            tt(t3, t0, t1, ALU.min).then_inc(S["gate_args"], 1)
            dve.wait_ge(S["gate_exps"], 1)
            tt(fcols[:, 0], t2, t3, ALU.add).then_inc(S["gate_rates"], 1)
            dve.wait_ge(S["gate_sums"], 1)
            order(ts(fcols[:, 1].rearrange("p t h -> p (t h)"), bank[1][:, 0:16], -1.0, None, ALU.mult))

            def proj_tiles(i, groups):
                return lambda g: sum_to(dve, g, i * 2 + (groups + g + 1), proj[:, bass.ds(i * 4 + 2 * g, 2), :])

            dve_body(dve, 0, 0, BODY, 4, proj_tiles(0, 0))
            with dve.Fori(1, 6) as i:
                dve_body(dve, i * BODY, i * 2, BODY, 4, proj_tiles(i, 0))
            dve.wait_ge(evacuated, phases["fox_in"][1])
            dve.wait_ge(S["pads_zeroed"], 1)
            order(tt(conv_u[:, :, 2:258], proj[:, 8:16, :], proj[:, 16:24, :], ALU.mult))
            with order.passes(0, 8, 4) as j:
                y = conv_y[:, bass.ds(j, 1), :]
                order(ts(y, conv_u[:, bass.ds(j, 1), 0:SEQ], cw_a_flat[:, bass.ds(j * 3, 1)], None, ALU.mult))
                for k in (1, 2):
                    order(stt(y, conv_u[:, bass.ds(j, 1), k:k + SEQ], cw_a_flat[:, bass.ds(j * 3 + k, 1)], y, ALU.mult, ALU.add))
                order(tt(y, y, proj[:, bass.ds(j, 1), :], ALU.mult))
            nc.vector.tensor_copy(stats[:, 7:8], stats[:, 0:1]).then_inc(S["conv_out"], 1)
            with dve.Fori(0, 6) as i:
                dve_body(dve, i * BODY + phases["fox_in"][0], i * 2 + phases["fox_in"][1], BODY, 4, proj_tiles(i, a_groups["fox_in"]))
            dve.wait_ge(evacuated, phases["ab_out"][1])
            heads = proj[:].rearrange("p (a h) s -> p a h s", a=3)
            with order.passes(0, FOX_HEADS, 4) as h:
                dve.wait_ge(S["qk_roots"], h + 1)
                order(nc.vector.reciprocal(f_rt, f_rt))
                stt(f_qk[:, 0:1, :], heads[:, 0, bass.ds(h, 1), :], q_bias, f_rt[:, 0:1, :], ALU.mult, ALU.mult)
                stt(f_qk[:, 1:2, :], heads[:, 1, bass.ds(h, 1), :], k_bias, f_rt[:, 1:2, :], ALU.mult,
                    ALU.mult).then_inc(S["qk_ready"], 1)
                dve.wait_ge(S["logits_done"], h + 1)
                stt(f_lg[:, 0, :], bank[2][:, 0:P], fcols_flat[:, bass.ds(h + 16, 1)], const("causal_mask"), ALU.add, ALU.add)
                order(stt(f_lg[:, 1:3, :].rearrange("p i c -> p (i c)"), bank[2][:, P:3 * P], fcols_flat[:, bass.ds(h + 24, 1)],
                          causal2, ALU.add, ALU.add))
                nc.vector.reduce_max(f_st[:, 0:1], f_lg[:, 0, :], AX_X)
                order(nc.vector.reduce_max(f_st[:, 1:2], f_lg[:, 1:3, :].rearrange("p i c -> p (i c)"), AX_X))
                ts(f_st[:, 2:4], f_st[:, 0:2], -1.0, None, ALU.mult).then_inc(S["max_ready"], 1)
                dve.wait_ge(S["exps_done"], h + 1)
                order(nc.vector.reciprocal(f_st[:, 6:8], f_st[:, 4:6]))
                ts(f_p[:, 0, :], f_p[:, 0, :], f_st[:, 6:7], None, ALU.mult)
                ts(f_p[:, 1:3, :], f_p[:, 1:3, :], f_st[:, 7:8], None, ALU.mult).then_inc(S["probs_ready"], 1)
                dve.wait_ge(S["fox_high"], h + 1)
                yt = yx[:, bass.ds(h + 8, 1), :, :]
                tt(yt[:, :, 1, :], bank[0][:, 0:SEQ].unsqueeze(1), yt[:, :, 0, :].bitcast(F32),
                   ALU.subtract).then_inc(S["fox_low"], 1)
            with dve.Fori(0, 2) as i:
                out_proj(i * 2 * BODY + phases["ab_out"][0], i * 2 + phases["ab_out"][1], i)

            def mlp(layer):
                base, cg = phases[f"mlp{layer}"]
                dve.wait_ge(evacuated, cg)
                norm(2 * layer + 1)

                def block_(b, end=False):
                    with dve.Fori(0, 4) as i:
                        def evac(g):
                            c = b * MLP_C + i * 2 + (cg + g + 1)
                            dve.wait_ge(S["mlp_low"], b * 8 + i * 2 + (8 * BLOCKS * layer + g + 1))
                            sum_to(dve, g, b * 8 + i * 2 + (a_groups[f"mlp{layer}"] + g + 1), mlp_sum[:, g])
                            dve.wait_ge(evacuated, c)
                            stt(mlp_sq[:, g], mlp_sum[:, g], 0.0, mlp_sum[:, g], ALU.max, ALU.mult).then_inc(S["squared"], 1)

                        dve_body(dve, b * MLP_P + i * BODY + base, b * MLP_C + i * 2 + cg, BODY, 4, evac)
                    def down(i, end=False):
                        out_proj(b * MLP_P + i * 2 * BODY + (base + 4 * BODY), b * MLP_C + i * 2 + (cg + 8), i, end)

                    if end:
                        down(0)
                        down(1, True)
                    else:
                        with dve.Fori(0, 2) as i:
                            down(i)

                with dve.Fori(0, BLOCKS - 1) as b:
                    block_(b)
                block_(BLOCKS - 1, end=layer == 1)

            mlp(0)
            gp, gc = phases["gdn"]
            dve.wait_ge(evacuated, gc)
            norm(2)
            small_low_parts(1, SMALL_N)
            dve.wait_ge(S["small_done"], 2)
            ps = bank[0][:, 0:2 * SMALL_N].rearrange("p (t n) -> p t n", t=TT)
            for t in range(TT):
                last = tt(g_t[:, 0, t, :], ps[:, t, V_HEADS:], small[:, 48:80], ALU.add)
            order(last)
            order(ts(g_t[:, 1], g_t[:, 0], -1.0, None, ALU.mult))
            ts(g_t[:, 2], g_t[:, 0], 0.0, None, ALU.max)
            ts(g_t[:, 4], ps[:, :, 0:V_HEADS], -1.0, None, ALU.mult)
            tt(g_t[:, 3], g_t[:, 0], g_t[:, 1], ALU.min).then_inc(S["gate_args"], 1)
            dve.wait_ge(S["gate_exps"], 2)
            order(tt(g_t[:, 2], g_t[:, 2], g_t[:, 3], ALU.add))
            for t in range(TT):
                last = stt(gcols[:, G, t, :], g_t[:, 2, t, :], -1.0, small[:, 16:48], ALU.mult, ALU.mult)
            last.then_inc(S["gate_rates"], 1)
            order(ts(g_t[:, 4], g_t[:, 4], 1.0, None, ALU.add))
            order(nc.vector.reciprocal(gcols[:, BETA], g_t[:, 4]))
            dve.wait_ge(S["gate_sums"], 2)
            flat = lambda a: a.rearrange("p t h -> p (t h)")
            order(ts(flat(gcols[:, NEGC]), bank[1][:, 0:64], -1.0, None, ALU.mult))
            tt(flat(g_t[:, 0]), bank[1][:, 64:128], flat(gcols[:, NEGC]), ALU.add).then_inc(S["gate_args"], 1)
            dve.wait_ge(S["gate_exp2"], 1)
            ts(gcols[:, NEGEXP], g_t[:, 1], -1.0, None, ALU.mult)
            order(tt(gcols[:, BLAST], g_t[:, 0], gcols[:, BETA], ALU.mult))

            def group_convs(g, half, g2):
                nc.vector.tensor_copy(gg[:].rearrange("p q t h -> p (q t) h"),
                                      gcols[:].rearrange("p q t h -> p (q t) h")[:, :, bass.ds(g * GV, GV)])
                nc.vector.tensor_copy(cw_grp[:, 0:GQ, :], cw_g[:, bass.ds(g * GQ, GQ), :])
                nc.vector.tensor_copy(cw_grp[:, GQ:2 * GQ, :], cw_g[:, bass.ds(g * GQ + QK_HEADS, GQ), :])
                nc.vector.tensor_copy(cw_grp[:, 2 * GQ:, :], cw_g[:, bass.ds(g * GV + 2 * QK_HEADS, GV), :]).then_inc(S["group_cols"], 1)
                dve.wait_ge(S["group_cols"], g + 1)

            def head(n, j):
                dve.wait_ge(S["qk_roots"], n + (1 + FOX_HEADS))
                order(nc.vector.reciprocal(d_rt, d_rt))
                stt(d_qk[:, 0, :], proj[:, j, :], HD ** -0.5, d_rt[:, 0, :], ALU.mult, ALU.mult)
                tt(d_qk[:, 1, :], proj[:, GQ + j, :], d_rt[:, 1, :], ALU.mult).then_inc(S["qk_ready"], 1)
                dve.wait_ge(S["sums_spread"], n + 1)
                for m in range(4):
                    e, t = m // 2, m % 2
                    last = stt(d_df[:, e, t, :], bank[1][:, m * P:(m + 1) * P], gg[:, NEGC, t, 2 * j + e:2 * j + e + 1],
                               const("decay_mask"), ALU.add, ALU.add)
                last.then_inc(S["decay_args"], 1)
                dve.wait_ge(S["decays_ready"], n + 1)
                dve.wait_ge(S["grams_done"], n + 1)
                for m in range(4):
                    e, t = m // 2, m % 2
                    last = stt(d_Lt[:, e, t, :], bank[3][:, 2 * t * P:(2 * t + 1) * P], gg[:, BETA, t, 2 * j + e:2 * j + e + 1],
                               d_D[:, e, t, :], ALU.mult, ALU.mult)
                last.then_inc(S["lower_ready"], 1)
                qk = bank[3].rearrange("p (t i c) -> p t i c", t=2, i=2)[:, :, 1, :]
                for e in range(2):
                    tt(d_Sc[:, e], qk, d_D[:, e], ALU.mult)
                    last = tt(d_qe[:, e, :], d_qk[:, 0, P:SEQ], d_qe[:, e, :], ALU.mult)
                last.then_inc(S["scores_ready"], 1)
                dve.wait_ge(S["lower_ready"], n + 1)
                flat4 = lambda a: a.rearrange("p e t c -> p (e t) c")
                wide = lambda name: const(name).unsqueeze(1).to_broadcast([P, 4, P])
                b4 = lambda i: bank[i].rearrange("p (m c) -> p m c", m=4)
                T, Tt, Lt, Y = (flat4(a) for a in (d_T, d_Tt, d_Lt, d_Y))
                order(tt(Tt, Lt, wide("sub1_t"), ALU.mult))
                tt(Tt, wide("ident"), Tt, ALU.subtract)
                dve.wait_ge(S["lower_turned"], n + 1)
                order(tt(Y, b4(1), wide("sub1"), ALU.mult))
                tt(T, wide("ident"), Y, ALU.subtract).then_inc(S["inverse_ready"], 1)
                for i, b in enumerate(LEVELS):
                    dve.wait_ge(S["product_done"], n * 6 + (i + 1))
                    tt(Y, b4(2), wide(f"sub{b}"), ALU.mult).then_inc(S["product_masked"], 1)
                    dve.wait_ge(S["update_done"], n * 6 + (i + 1))
                    if i < len(LEVELS) - 1:
                        tt(T, T, b4(0), ALU.subtract)
                    tt(Tt, Tt, b4(3), ALU.subtract).then_inc(S["inverse_ready"], 1)
                dve.wait_ge(S["read_done"], n + 1)
                for e in range(2):
                    last = stt(d_R[:, e, :], bank[0][:, e * P:(e + 1) * P], gg[:, NEGEXP, 1, 2 * j + e:2 * j + e + 1],
                               d_Vt[:, e, 1, :], ALU.mult, ALU.add)
                last.then_inc(S["rhs1_ready"], 1)
                dve.wait_ge(S["o_roots"], n + 1)
                order(nc.vector.reciprocal(d_rt, d_rt))
                order(tt(d_y.rearrange("p a s -> p (a s)"), bank[3], d_rt.rearrange("p a s -> p (a s)"), ALU.mult))
                stt(d_y, d_y, small[:, 2:3], proj[:, 16 + 2 * j:18 + 2 * j, :], ALU.mult, ALU.mult).then_inc(S["y_ready"], 1)
                dve.wait_ge(S["y_low"], n + 1)

            with order.passes(0, 2, 2 * PER_GROUP) as half:
                with order.passes(0, 2, PER_GROUP) as g2:
                    group_convs(half * 2 + g2, half, g2)
                    for b in range(6):
                        p0, cg0 = half * HALF_P + g2 * GRP_P + (gp + b * BODY), half * HALF_C + g2 * GRP_C + (gc + 2 * b)

                        def evac(g):
                            groups = half * 24 + g2 * 12 + (a_groups["gdn"] + 2 * b + g + 1)
                            dve.wait_ge(S["activated"], half * 24 + g2 * 12 + 2 * b + g + 1)
                            if b >= 4:
                                sum_to(dve, g, groups, d_c)
                                return
                            sum_to(dve, g, groups, d_u[:, :, 3:259])
                            dve.wait_ge(evacuated, cg0 + g + 1)
                            for k in range(4):
                                for i in range(2):
                                    w = cw_grp[:, 4 * b + 2 * g + i, k:k + 1]
                                    if k == 0:
                                        last = ts(d_c[:, i, :], d_u[:, i, 0:SEQ], w, None, ALU.mult)
                                    else:
                                        last = stt(d_c[:, i, :], d_u[:, i, k:k + SEQ], w, d_c[:, i, :], ALU.mult, ALU.add)
                                if k < 3:
                                    order(last)
                            last.then_inc(S["convolved"], 1)

                        dve_body(dve, p0, cg0, BODY, 4, evac)
                    for j in range(GQ):
                        head(half * (2 * GQ) + g2 * GQ + j, j)
                with dve.Fori(0, 2) as i:
                    out_proj(half * HALF_P + i * 2 * BODY + (gp + 2 * GRP_P), half * HALF_C + i * 2 + (gc + 2 * GRP_C), i)
            mlp(1)

        @block.gpsimd
        def _(pool):
            tt = nc.gpsimd.tensor_tensor
            nc.gpsimd.memset(conv_u[:, :, 0:2], 0.0)
            nc.gpsimd.memset(d_u[:, :, 0:3], 0.0)
            nc.gpsimd.memset(eps_col, EPS).then_inc(S["pads_zeroed"], 1)
            nc.gpsimd.memset(small[:, 84:86], -0.5).then_inc(S["mlp_low"], 2)

            def norm(n):
                pool.wait_ge(S["mean_ready"], n + 1)
                tt(stats[:, 4:6], stats[:, 2:4], small[:, 84:86], ALU.pow).then_inc(S["rstd_ready"], 1)

            def low_part(out_h, out_l, src, name):
                tt(out_l, src, out_h.bitcast(F32), ALU.subtract).then_inc(S[name], 1)

            pool.wait_ge(S["mlp_low"], 2)
            norm(0)
            pool.wait_ge(S["conv_high"], 1)
            low_part(yx[:, 0:8, 0, :], yx[:, 0:8, 1, :], conv_y, "conv_low")
            with pool.Fori(0, FOX_HEADS) as h:
                if True:
                    src = fcols[:, 0, :, bass.ds(h, 1)].to_broadcast([P, TT, P])
                    nc.gpsimd.tensor_copy(f_lf, src).then_inc(S["logit_rows"], 1)
                pool.wait_ge(S["fox_low"], h + 1)

            def mlp(layer):
                norm(2 * layer + 1)
                with pool.Fori(0, BLOCKS) as b:
                    with pool.Fori(0, 4) as i:
                        for g in range(2):
                            pool.wait_ge(S["mlp_high"], b * 8 + i * 2 + (8 * BLOCKS * layer + g + 1))
                            tiles = yx[:, bass.ds(i * 4 + 2 * g, 2), :, :]
                            low_part(tiles[:, :, 0, :], tiles[:, :, 1, :], mlp_sq[:, g], "mlp_low")

            mlp(0)
            norm(2)
            with pool.Fori(0, 2) as half:
                with pool.Fori(0, 2) as g2:
                    pool.wait_ge(S["group_cols"], half * 2 + g2 + 1)
                    for j in range(GQ):
                        n = half * (2 * GQ) + g2 * GQ + j
                        src = gg[:, G, :, 2 * j:2 * j + 2].rearrange("p t e -> p e t").unsqueeze(3).to_broadcast([P, 2, TT, P])
                        if j == 0:
                            pool.wait_ge(S["activated"], half * 24 + g2 * 12 + 13)
                        for e in range(2):
                            last = tt(d_gb[:, e], src[:, e], const("ones").unsqueeze(1).to_broadcast([P, TT, P]), ALU.mult)
                        last.then_inc(S["g_spread"], 1)
                        pool.wait_ge(S["y_high"], n + 1)
                        tiles = yx[:, bass.ds(g2 * 8 + 2 * j, 2), :, :]
                        low_part(tiles[:, :, 0, :], tiles[:, :, 1, :], d_y, "y_low")
            mlp(1)


_INS = ["x", "norm_mix", "norm_mlp", "w_mlp_in", "w_mlp_out", "ab_w_in", "ab_conv_w", "fox_f_bias", "fox_q_norm",
        "fox_k_norm", "ab_w_out", "gdn_w_in", "gdn_conv_w", "gdn_a_log", "gdn_dt_bias", "gdn_out_norm", "gdn_w_out"]


def kernel(**inputs):
    import concourse.bacc as bacc
    from concourse.bass_utils import run_bass_kernel_spmd

    nc = bacc.Bacc("TRN2", target_bir_lowering=False, num_devices=1)
    arrays, args = {}, []
    given = [(name, np.ascontiguousarray(inputs[name])) for name in _INS] + [("consts", shape_constants())]
    for name, a in given:
        arrays[f"in_{name}_dram"] = a
        args.append(nc.dram_tensor(f"in_{name}_dram", a.shape, mybir.dt.from_np(a.dtype), kind="ExternalInput").ap())
    out = nc.dram_tensor("out_0_dram", (1, SEQ, D), F32, kind="ExternalOutput").ap()
    trunk(nc, *args, out)
    r = run_bass_kernel_spmd(nc, [arrays], core_ids=[0])
    return r.results[0]["out_0_dram"]
```
